# Optimizing a Trainium2 kernel written in Bass

```python
import jax, jax.numpy as jnp
from jax import lax
import numpy as np

D_MODEL = 1024
BATCH = 1
SEQ = 1024
DEPTH = 1
DEC_BATCH = 8
DEC_SEQ = 16
PAST_LEN = 128

CHUNK = 64
W_A = 512
CONV_A_WIDTH = 3
N_HEADS = 4
HEAD_K = 128
HEAD_V = 128
W_QK = N_HEADS * HEAD_K
W_VV = N_HEADS * HEAD_V
W_QKV = 2 * W_QK + W_VV
CONV_QKV_WIDTH = 4
D_FF = 4 * D_MODEL
IN_SIZES = (W_A, W_A, W_A, W_QKV, W_VV, N_HEADS, N_HEADS, D_MODEL, D_MODEL)
IN_WIDTH = 3 * W_A + W_QKV + W_VV + 2 * N_HEADS + 2 * D_MODEL
EPS = 1e-6

kernel_name = "hybrid_stream_gconv_gdn_step"

def _in_offsets():
    offs, acc = [], 0
    for s in IN_SIZES[:-1]:
        acc += s
        offs.append(acc)
    return offs

def rmsnorm(x, g):
    xf = x.astype(jnp.float32)
    y = xf * lax.rsqrt(jnp.mean(xf * xf, axis=-1, keepdims=True) + EPS)
    return (y * g.astype(jnp.float32)).astype(x.dtype)

def l2norm(x):
    xf = x.astype(jnp.float32)
    return xf * lax.rsqrt(jnp.sum(xf * xf, axis=-1, keepdims=True) + EPS)

def causal_conv(x, buf, w):
    width = w.shape[0]
    L = x.shape[1]
    xp = jnp.concatenate([buf.astype(x.dtype), x], axis=1)
    y = xp[:, 0:L] * w[0]
    for i in range(1, width):
        y = y + xp[:, i:i + L] * w[i]
    return y, xp[:, xp.shape[1] - (width - 1):]

def gated_delta_rule(q, k, v, beta, g, S0, chunk):
    Bn, L, H, K = q.shape
    V = v.shape[-1]
    N = L // chunk
    f32 = jnp.float32

    def blk(t):
        t = t.astype(f32).reshape((Bn, N, chunk, H) + t.shape[3:])
        return jnp.moveaxis(t, 3, 1)

    q, k, v, beta, g = blk(q), blk(k), blk(v), blk(beta), blk(g)
    gc = jnp.cumsum(g, axis=-1)
    incl = jnp.tril(jnp.ones((chunk, chunk), dtype=bool))
    strict = jnp.tril(jnp.ones((chunk, chunk), dtype=bool), k=-1)
    diff = gc[..., :, None] - gc[..., None, :]
    decay = jnp.exp(jnp.where(incl, diff, -jnp.inf))
    kk = jnp.einsum('bhnik,bhnjk->bhnij', k, k)
    A = jnp.where(strict, kk * decay * beta[..., :, None], 0.0)
    eye = jnp.eye(chunk, dtype=f32)
    rhs = jnp.concatenate([v * beta[..., None], k * (beta * jnp.exp(gc))[..., None]], axis=-1)
    sol = lax.linalg.triangular_solve(eye + A, rhs, left_side=True, lower=True,
                                      unit_diagonal=True)
    w_v, w_k = sol[..., :V], sol[..., V:]
    P = jnp.einsum('bhnik,bhnjk->bhnij', q, k) * decay
    q_g = q * jnp.exp(gc)[..., None]
    k_t = k * jnp.exp(gc[..., -1:] - gc)[..., None]
    g_last = jnp.exp(gc[..., -1])

    def step(S, inp):
        wv, wk, Pb, qg, kt, gl = inp
        U = wv - jnp.einsum('bhck,bhkv->bhcv', wk, S)
        o = jnp.einsum('bhck,bhkv->bhcv', qg, S) + jnp.einsum('bhcd,bhdv->bhcv', Pb, U)
        S = S * gl[..., None, None] + jnp.einsum('bhck,bhcv->bhkv', kt, U)
        return S, o

    xs = tuple(jnp.moveaxis(t, 2, 0) for t in (w_v, w_k, P, q_g, k_t, g_last))
    S_fin, o = lax.scan(step, S0.astype(f32), xs)
    o = jnp.transpose(o, (1, 0, 3, 2, 4)).reshape(Bn, L, H, V)
    return o, S_fin

def hybrid_layer(x, buf_a, buf_qkv, S0, chunk, norm1_g, w_in, conv_a_w, w_a_out,
                 conv_qkv_w, a_log, dt_bias, onorm_g, w_b_out, w_o, norm2_g, w_up, w_down):
    Bn, L, _ = x.shape
    xn = rmsnorm(x, norm1_g)
    proj = xn @ w_in
    b_a, c_a, x_a, qkv, z, beta_raw, a_raw, gate_a, gate_b = jnp.split(proj, _in_offsets(), axis=-1)

    u, new_buf_a = causal_conv(c_a * x_a, buf_a, conv_a_w)
    y_a = (b_a * u) @ w_a_out

    qkv_c, new_buf_qkv = causal_conv(qkv, buf_qkv, conv_qkv_w)
    qkv_c = jax.nn.silu(qkv_c)
    q, k, v = jnp.split(qkv_c, [W_QK, 2 * W_QK], axis=-1)
    q = l2norm(q.reshape(Bn, L, N_HEADS, HEAD_K)) * (HEAD_K ** -0.5)
    k = l2norm(k.reshape(Bn, L, N_HEADS, HEAD_K))
    v = v.reshape(Bn, L, N_HEADS, HEAD_V).astype(jnp.float32)
    beta = jax.nn.sigmoid(beta_raw.astype(jnp.float32))
    g = -jnp.exp(a_log.astype(jnp.float32)) * jax.nn.softplus(
        a_raw.astype(jnp.float32) + dt_bias.astype(jnp.float32))
    o, S_new = gated_delta_rule(q, k, v, beta, g, S0, chunk)
    o = rmsnorm(o, onorm_g) * jax.nn.silu(z.reshape(Bn, L, N_HEADS, HEAD_V).astype(jnp.float32))
    y_b = o.reshape(Bn, L, W_VV).astype(x.dtype) @ w_b_out

    mixed = jax.nn.sigmoid(gate_a) * y_a + jax.nn.sigmoid(gate_b) * y_b
    h = x + mixed @ w_o
    f = jnp.square(jax.nn.relu(rmsnorm(h, norm2_g) @ w_up)) @ w_down
    return h + f, new_buf_a, new_buf_qkv, S_new

def run_trunk(x, bufs_a, bufs_qkv, Ss, chunk, norm1_g, w_in, conv_a_w, w_a_out,
              conv_qkv_w, a_log, dt_bias, onorm_g, w_b_out, w_o, norm2_g, w_up, w_down,
              final_g):
    na, nq, ns = [], [], []
    for l in range(DEPTH):
        x, ba, bq, S = hybrid_layer(x, bufs_a[l], bufs_qkv[l], Ss[l], chunk, norm1_g[l], w_in[l],
                                    conv_a_w[l], w_a_out[l], conv_qkv_w[l], a_log[l], dt_bias[l],
                                    onorm_g[l], w_b_out[l], w_o[l], norm2_g[l], w_up[l], w_down[l])
        na.append(ba)
        nq.append(bq)
        ns.append(S)
    return rmsnorm(x, final_g), jnp.stack(na), jnp.stack(nq), jnp.stack(ns)

def setup_inputs(seed: int = 0) -> dict:
    key = jax.random.key(seed)
    ks = jax.random.split(key, 24)
    f32 = jnp.float32
    nrm = lambda k, s, sc: jax.random.normal(k, s, f32) * sc
    dt = jnp.exp(jax.random.uniform(ks[10], (DEPTH, N_HEADS), f32, np.log(1e-3), np.log(1e-1)))
    return {
        "x_prompt": nrm(ks[0], (BATCH, SEQ, D_MODEL), 1.0),
        "x_sample": nrm(ks[1], (DEC_BATCH, DEC_SEQ, D_MODEL), 1.0),
        "state_conv_a": nrm(ks[2], (DEPTH, DEC_BATCH, CONV_A_WIDTH - 1, W_A), 1.0),
        "state_conv_qkv": nrm(ks[3], (DEPTH, DEC_BATCH, CONV_QKV_WIDTH - 1, W_QKV), 1.0),
        "state_delta": nrm(ks[4], (DEPTH, DEC_BATCH, N_HEADS, HEAD_K, HEAD_V), HEAD_K ** -0.5),
        "norm1_g": 1.0 + nrm(ks[5], (DEPTH, D_MODEL), 0.02),
        "w_in": nrm(ks[6], (DEPTH, D_MODEL, IN_WIDTH), D_MODEL ** -0.5),
        "conv_a_w": nrm(ks[7], (DEPTH, CONV_A_WIDTH, W_A), CONV_A_WIDTH ** -0.5),
        "w_a_out": nrm(ks[8], (DEPTH, W_A, D_MODEL), W_A ** -0.5),
        "conv_qkv_w": nrm(ks[9], (DEPTH, CONV_QKV_WIDTH, W_QKV), CONV_QKV_WIDTH ** -0.5),
        "a_log": jnp.log(jax.random.uniform(ks[11], (DEPTH, N_HEADS), f32, 1.0, 16.0)),
        "dt_bias": dt + jnp.log(-jnp.expm1(-dt)),
        "onorm_g": 1.0 + nrm(ks[12], (DEPTH, HEAD_V), 0.02),
        "w_b_out": nrm(ks[13], (DEPTH, W_VV, D_MODEL), W_VV ** -0.5),
        "w_o": nrm(ks[14], (DEPTH, D_MODEL, D_MODEL), D_MODEL ** -0.5),
        "norm2_g": 1.0 + nrm(ks[15], (DEPTH, D_MODEL), 0.02),
        "w_up": nrm(ks[16], (DEPTH, D_MODEL, D_FF), D_MODEL ** -0.5),
        "w_down": nrm(ks[17], (DEPTH, D_FF, D_MODEL), D_FF ** -0.5),
        "final_g": 1.0 + nrm(ks[18], (D_MODEL,), 0.02),
    }

def reference(x_prompt, x_sample, state_conv_a, state_conv_qkv, state_delta, norm1_g, w_in,
              conv_a_w, w_a_out, conv_qkv_w, a_log, dt_bias, onorm_g, w_b_out, w_o, norm2_g,
              w_up, w_down, final_g):
    nb = x_prompt.shape[0]
    zero_a = jnp.zeros((DEPTH, nb, CONV_A_WIDTH - 1, W_A), x_prompt.dtype)
    zero_qkv = jnp.zeros((DEPTH, nb, CONV_QKV_WIDTH - 1, W_QKV), x_prompt.dtype)
    zero_S = jnp.zeros((DEPTH, nb, N_HEADS, HEAD_K, HEAD_V), jnp.float32)
    y_prompt, p_a, p_qkv, p_S = run_trunk(
        x_prompt, zero_a, zero_qkv, zero_S, CHUNK, norm1_g, w_in, conv_a_w, w_a_out,
        conv_qkv_w, a_log, dt_bias, onorm_g, w_b_out, w_o, norm2_g, w_up, w_down, final_g)
    y_sample, s_a, s_qkv, s_S = run_trunk(
        x_sample, state_conv_a, state_conv_qkv, state_delta, x_sample.shape[1], norm1_g, w_in,
        conv_a_w, w_a_out, conv_qkv_w, a_log, dt_bias, onorm_g, w_b_out, w_o, norm2_g, w_up,
        w_down, final_g)
    return (y_prompt, y_sample,
            p_a.astype(state_conv_a.dtype), p_qkv.astype(state_conv_qkv.dtype),
            p_S.astype(state_delta.dtype),
            s_a.astype(state_conv_a.dtype), s_qkv.astype(state_conv_qkv.dtype),
            s_S.astype(state_delta.dtype))


_drawn_inputs = setup_inputs


def setup_inputs(seed=0):
    import zlib

    import numpy as np

    out = dict(_drawn_inputs(seed))
    spreads = {}
    factors = {'onorm_g': 8.0, 'norm2_g': 3.423, 'final_g': 2.896}
    for name, (base, spread) in spreads.items():
        noise = np.random.default_rng([zlib.crc32(name.encode()), seed]).standard_normal(out[name].shape)
        drawn = base * np.exp(spread * noise) if base else spread * noise
        out[name] = __import__('jax').numpy.asarray(drawn.astype(out[name].dtype))
    for name, factor in factors.items():
        out[name] = (out[name] * factor).astype(out[name].dtype)
    return out
```

```python
from contextlib import ExitStack

import numpy as np

import concourse.bass as bass
from concourse import mybir

ACT = mybir.ActivationFunctionType
ALU = mybir.AluOpType
F32 = mybir.dt.float32
F32R = mybir.dt.float32r

P = 128
D = 1024
KD = D // P
ROWS_P, STREAMS, SLEN = 1024, 8, 16
ROWS = ROWS_P + STREAMS * SLEN
RT = ROWS // P
NT = 3
NW = ROWS // NT
WA = 512
TA = WA // P
H = 4
WQKV = 1536
TQ = WQKV // P
COL_QKV, COL_Z, COL_BA = 3 * WA, 3 * WA + WQKV, 3 * WA + WQKV + 512
COL_GA = COL_BA + 2 * H
COL_GB = COL_GA + D
FF = 4096
FC = 512
NFC = FF // FC
EPS = 1e-6
LEVELS = 7
LEVELS_S = 4
NEG = -1.0e30

C_ID, C_ONE, C_INC, C_NEG, C_STR, C_BLK, C_LEV = 0, 128, 256, 512, 768, 1024, 1152
C_SEQ = C_LEV + LEVELS * P
C_END = C_SEQ + STREAMS
V_G1, V_G2, V_CQ, V_CA, V_ON = 0, KD, 2 * KD, 2 * KD + 4 * TQ, 2 * KD + 4 * TQ + 3 * TA
V_END = V_ON + 1


def constants():
    c = np.zeros((P, C_END), np.float32)
    j, i = np.arange(P)[:, None], np.arange(P)[None, :]
    c[:, C_ID:C_ID + P] = i == j
    c[:, C_ONE:C_ONE + P] = 1
    same = (i // SLEN) == (j // SLEN)
    for n, block in enumerate((np.ones((P, P), bool), same)):
        c[:, C_INC + n * P:C_INC + (n + 1) * P] = (j <= i) & block
        c[:, C_NEG + n * P:C_NEG + (n + 1) * P] = np.where((j <= i) & block, 0, NEG)
        c[:, C_STR + n * P:C_STR + (n + 1) * P] = (j < i) & block
    c[:, C_BLK:C_BLK + P] = same
    for n in range(LEVELS):
        b = 2 ** n
        below = (j // b % 2 == 1) & (j // b == i // b + 1)
        c[:, C_LEV + n * P:C_LEV + (n + 1) * P] = below | (i == j)
    c[:, C_SEQ:C_END] = j // SLEN == np.arange(STREAMS)[None, :]
    return c


def padded(width):
    h = width - 1
    return h + ROWS_P + STREAMS * (h + SLEN), h + ROWS_P


class Memory:

    def __init__(self, nc):
        base = -(-nc.sbuf_base // 64) * 64
        self.const = base
        self.xn = base + 11264
        self.q = self.xn + 2 * KD * ROWS * 4
        self.k = self.q + H * ROWS * 4
        self.v = self.k + H * ROWS * 4
        self.t = self.v + H * ROWS * 4
        self.h = nc.sbuf_usable_end // 64 * 64 - RT * D * 4
        assert self.h >= self.t + 34000, (self.h, self.t)


def build(nc, x_prompt, x_sample, state_conv_a, state_conv_qkv, state_delta, norm1_g, w_in, conv_a_w,
          w_a_out, conv_qkv_w, a_log, dt_bias, onorm_g, w_b_out, w_o, norm2_g, w_up, w_down, final_g,
          table, y_prompt, y_sample, p_conv_a, p_conv_qkv, p_delta, s_conv_a, s_conv_qkv, s_delta):
    mem = Memory(nc)
    n_names = [0]

    def at(name, shape, dt, offset):
        n_names[0] += 1
        return nc.alloc_sbuf_tensor_at(f"{name}_{n_names[0]}", shape, dt, offset=offset)

    with ExitStack() as stack:
        ps = stack.enter_context(nc.psum_tensor("ps", [P, 8, 512], F32))
        off = [mem.const]

        def keep(name, *shape):
            a = at(name, [P, *shape], F32, off[0])
            off[0] += -(-int(np.prod(shape)) * 4 // 32) * 32
            assert off[0] <= mem.xn, (off[0], mem.xn)
            return a

        con = keep("con", C_END)
        vec = keep("vec", V_END)
        ba = keep("ba", RT, 2 * H)
        stat = keep("stat", 4, RT)
        half = keep("half", 80)
        hist_q = keep("hist_q", TQ, STREAMS * 3)
        hist_a = keep("hist_a", TA, STREAMS * 2)
        xn_hi = at("xn_hi", [P, KD, ROWS], F32R, mem.xn)
        xn_lo = at("xn_lo", [P, KD, ROWS], F32R, mem.xn + KD * ROWS * 4)
        rows = at("rows", [P, RT, D], F32, mem.h)
        qkv = at("qkv", [P, 3 * H, ROWS], F32, mem.q)
        ident = con[:, C_ID:C_ID + P]
        ones = con[:, C_ONE:C_ONE + P]

        b = Builder(nc, stack, ps, at, mem, con, vec, ba, stat, half, hist_q, hist_a, xn_hi, xn_lo,
                    rows, qkv, ident, ones)
        b.setup(table, norm1_g, norm2_g, conv_qkv_w, conv_a_w, onorm_g, state_conv_qkv, state_conv_a,
                x_prompt, x_sample)
        b.norm(V_G1)
        b.project_qkv(w_in)
        b.states_out(4, TQ, p_conv_qkv, s_conv_qkv)
        b.delta(a_log, dt_bias, state_delta, p_delta, s_delta)
        b.recycle()
        b.gate_o(w_in)
        b.merge("b", w_in, w_b_out)
        b.branch_a(w_in)
        b.states_out(3, TA, p_conv_a, s_conv_a)
        b.merge("a", w_in, w_a_out)
        b.recycle()
        b.residual(w_o, x_prompt, x_sample)
        b.norm(V_G2)
        b.mlp(w_up, w_down)
        b.final(final_g, y_prompt, y_sample)


class Builder:
    def __init__(self, nc, stack, ps, at, mem, con, vec, ba, stat, half, hist_q, hist_a, xn_hi, xn_lo,
                 rows, qkv, ident, ones):
        self.nc, self.stack, self.ps, self.at, self.mem = nc, stack, ps, at, mem
        self.con, self.vec, self.ba, self.stat, self.half = con, vec, ba, stat, half
        self.hist_q, self.hist_a, self.xn_hi, self.xn_lo = hist_q, hist_a, xn_hi, xn_lo
        self.rows, self.qkv, self.ident, self.ones = rows, qkv, ident, ones
        self.n_sems, self.live = 0, []

    def sems(self, *names):
        self.n_sems += 1
        made = [self.nc.alloc_semaphore(name=f"{n}_{self.n_sems}") for n in names]
        self.live += made
        return made

    def recycle(self):
        self.nc.clear_and_free_semaphores(self.live)
        self.live = []
        self.nc.all_engine_barrier()

    def three(self, s):
        return self.ps[:, 3 * s:3 * s + 3, 0:NW]

    def product(self, out_set, k_tiles, w_hi, w_lo, x_hi, x_lo):
        nc = self.nc
        for g in range(NT):
            rows = slice(g * NW, (g + 1) * NW)
            for k in range(k_tiles):
                for n, (w, x) in enumerate(((w_hi, x_hi), (w_hi, x_lo), (w_lo, x_hi))):
                    last = nc.tensor.matmul(self.ps[:, 3 * out_set + g, 0:NW], w(k), x[:, k, rows],
                                            start=(k == 0 and n == 0), stop=(k == k_tiles - 1 and n == 2))
        return last

    def setup(self, table, norm1_g, norm2_g, conv_qkv_w, conv_a_w, onorm_g, state_conv_qkv,
              state_conv_a, x_prompt, x_sample):
        nc, ps = self.nc, self.ps
        vrow = self.at("vrow", [V_END, P], F32, self.mem.t)
        qrow = self.at("qrow", [STREAMS * 3, WQKV], F32, self.mem.q)
        arow = self.at("arow", [STREAMS * 2, WA], F32, self.mem.k)
        loaded, x_in, turned, moved, half_set = self.sems("loaded", "x_in", "turned", "moved", "half_set")
        with nc.Block() as block:
            @block.sync
            def _(sp):
                sp.dma_start(self.con[:, :], table[:, :]).then_inc(loaded, 16)
                for col, src in ((V_G1, norm1_g.rearrange("l (f p) -> (l f) p", p=P)),
                                 (V_G2, norm2_g.rearrange("l (f p) -> (l f) p", p=P)),
                                 (V_CQ, conv_qkv_w.rearrange("l w (f p) -> (l w f) p", p=P)),
                                 (V_CA, conv_a_w.rearrange("l w (f p) -> (l w f) p", p=P)),
                                 (V_ON, onorm_g)):
                    sp.dma_start(vrow[col:col + src.shape[0], :], src).then_inc(loaded, 16)
                sp.dma_start(qrow[:, :], state_conv_qkv.rearrange("l s t c -> (l s t) c")).then_inc(loaded, 16)
                sp.dma_start(arow[:, :], state_conv_a.rearrange("l s t c -> (l s t) c")).then_inc(loaded, 16)
                sp.dma_start(self.rows[:, 0:RT - 1, :],
                             x_prompt[0].rearrange("(r p) d -> p r d", p=P)).then_inc(x_in, 16)
                sp.dma_start(self.rows[:, RT - 1, :], x_sample.rearrange("s t d -> (s t) d")).then_inc(x_in, 16)
                sp.wait_ge(x_in, 32)

            @block.tensor
            def _(pe):
                pe.wait_ge(loaded, 16 * 8)
                nc.tensor.transpose(ps[:, 0, 0:V_END], vrow[:, :], self.con[0:V_END, C_ID:C_ID + V_END])
                for f in range(TQ):
                    nc.tensor.transpose(ps[:, 1, f * 24:f * 24 + 24], qrow[:, f * P:(f + 1) * P],
                                        self.con[0:24, C_ID:C_ID + 24])
                for f in range(TA):
                    last = nc.tensor.transpose(ps[:, 2, f * 16:f * 16 + 16], arow[:, f * P:(f + 1) * P],
                                               self.con[0:16, C_ID:C_ID + 16])
                last.then_inc(turned, 1)

            @block.vector
            def _(dve):
                nc.vector.memset(self.half[:, 0:44], -0.5).then_inc(half_set, 1)
                nc.vector.memset(self.half[:, 44:80], 0.5).then_inc(half_set, 1)
                dve.wait_ge(turned, 1)
                nc.vector.tensor_copy(self.vec[:, :], ps[:, 0, 0:V_END]).then_inc(moved, 1)
                nc.vector.tensor_copy(self.hist_q[:, :, :],
                                      ps[:, 1, 0:TQ * 24].rearrange("p (f t) -> p f t", t=24)).then_inc(moved, 1)
                nc.vector.tensor_copy(self.hist_a[:, :, :],
                                      ps[:, 2, 0:TA * 16].rearrange("p (f t) -> p f t", t=16)).then_inc(moved, 1)

    def norm(self, gain):
        nc, ps, stat = self.nc, self.ps, self.stat
        scaled = self.at("scaled", [P, RT, D], F32, self.mem.q)
        junk = self.at("junk", [P, D], F32, self.mem.t)
        squared, mean, rooted, ready, turned, hi_done, lo_done = self.sems(
            "squared", "mean", "rooted", "scaled_ready", "turned", "hi_done", "lo_done")
        with nc.Block() as block:
            @block.scalar
            def _(act):
                for r in range(RT):
                    if r:
                        act.wait_ge(squared, r)
                    nc.scalar.activation(junk[:, :], self.rows[:, r, :], ACT.Square,
                                         accum_out=stat[:, 0, r:r + 1]).then_inc(squared, 1)

                with act.Fori(0, KD) as f:
                    for g in range(NT):
                        act.wait_ge(turned, NT * f + g + 1)
                        nc.scalar.activation(self.xn_hi[:, bass.ds(f, 1), g * NW:(g + 1) * NW], ps[:, g:g + 1, 0:NW],
                                             ACT.Copy, scale=self.vec[:, bass.ds(f + gain, 1)]).then_inc(hi_done, 1)

            @block.gpsimd
            def _(pool):
                for r in range(RT):
                    pool.wait_ge(mean, r + 1)
                    nc.gpsimd.tensor_tensor(stat[:, 2, r:r + 1], stat[:, 1, r:r + 1], self.half[:, 0:1],
                                            ALU.pow).then_inc(rooted, 1)

            @block.vector
            def _(dve):
                for r in range(RT):
                    dve.wait_ge(squared, r + 1)
                    nc.vector.tensor_scalar(stat[:, 1, r:r + 1], stat[:, 0, r:r + 1], 1.0 / D, EPS,
                                            ALU.mult, ALU.add).then_inc(mean, 1)
                for r in range(RT):
                    dve.wait_ge(rooted, r + 1)
                    nc.vector.tensor_scalar(scaled[:, r, :], self.rows[:, r, :], stat[:, 2, r:r + 1], None,
                                            ALU.mult).then_inc(ready, 1)

                with dve.Fori(0, KD) as f:
                    for g in range(NT):
                        dve.wait_ge(hi_done, NT * f + g + 1)
                        nc.vector.scalar_tensor_tensor(
                            self.xn_lo[:, bass.ds(f, 1), g * NW:(g + 1) * NW], ps[:, g:g + 1, 0:NW],
                            self.vec[:, bass.ds(f + gain, 1)],
                            self.xn_hi[:, bass.ds(f, 1), g * NW:(g + 1) * NW].bitcast(F32),
                            ALU.mult, ALU.subtract).then_inc(lo_done, 1)

            @block.tensor
            def _(pe):
                for f in range(KD):
                    for g in range(NT):
                        if f == 0:
                            pe.wait_ge(ready, 3 * g + 3)
                        else:
                            pe.wait_ge(lo_done, NT * (f - 1) + g + 1)
                        for r in range(3):
                            last = nc.tensor.transpose(ps[:, g, r * P:(r + 1) * P],
                                                       scaled[:, 3 * g + r, f * P:(f + 1) * P], self.ident)
                        last.then_inc(turned, 1)

    def ring(self, slots, raw_at, split_at):
        raw = self.at("w_raw", [P, slots, 1024], F32, raw_at)
        hi = self.at("w_hi", [P, slots, 1024], F32R, split_at)
        lo = self.at("w_lo", [P, slots, 1024], F32R, split_at + slots * 4096)
        return raw, hi, lo

    def round_hi(self, raw, hi, slot, hi_done):
        self.nc.scalar.copy(hi[:, slot, :], raw[:, slot, :]).then_inc(hi_done, 1)

    def take_lo(self, raw, hi, lo, slot, lo_done):
        self.nc.vector.tensor_tensor(lo[:, slot, :], raw[:, slot, :], hi[:, slot, :].bitcast(F32),
                                     ALU.subtract).then_inc(lo_done, 1)

    def project_qkv(self, w_in):
        nc, ps = self.nc, self.ps
        L, S0 = padded(4)
        A = L - 3
        t = self.mem.t
        raw, hi, lo = self.ring(2, t, t + 8192)
        pre = self.at("pre", [P, L], F32, t + 24576)
        acc = self.at("acc", [P, L], F32, t + 24576 + 4736)
        th = self.at("th", [P, L], F32, t + 24576 + 2 * 4736)
        w8 = self.at("w8", [P, KD, 2 * H], F32, t + 24576 + 3 * 4736)
        w8_hi = self.at("w8_hi", [P, KD, 2 * H], F32R, t + 24576 + 3 * 4736 + 256)
        w8_lo = self.at("w8_lo", [P, KD, 2 * H], F32R, t + 24576 + 3 * 4736 + 512)
        self.tail = self.at("tail_q", [P, TQ, 27], F32, self.mem.h + 20000)
        raw_ready = self.sems("raw_ready0", "raw_ready1")
        (w8_in, w8_split, ba_done, ba_out, hi_done, lo_done, projected, pre_done, cleared, conv, tanh_done,
         out_done) = self.sems("w8_in", "w8_split", "ba_done", "ba_out", "hi_done", "lo_done", "projected",
                               "pre_done", "cleared", "conv", "tanh_done", "out_done")
        STEPS = 7
        cols = w_in[0].rearrange("(k p) c -> p k c", p=P)

        def streams(buf):
            return buf[:, S0:L].rearrange("p (s t) -> p s t", t=3 + SLEN)

        with nc.Block() as block:
            @block.sync
            def _(sp):
                def load(tile, slot):
                    sp.dma_start(raw[:, slot, :].rearrange("p (k c) -> p k c", c=P),
                                 cols[:, :, bass.ds(tile * P + COL_QKV, P)]).then_inc(raw_ready[slot], 16)

                sp.dma_start(w8[:, :, :], cols[:, :, COL_BA:COL_BA + 2 * H]).then_inc(w8_in, 16)
                load(0, 0)
                load(1, 1)
                with sp.Fori(1, TQ // 2) as i:
                    for s in range(2):
                        sp.wait_ge(lo_done, 2 * i + s - 1)
                        load(2 * i + s, s)

            @block.scalar
            def _(act):
                act.wait_ge(w8_in, 16)
                nc.scalar.copy(w8_hi[:, :, :], w8[:, :, :]).then_inc(w8_split, 1)

                def split(i, s):
                    act.wait_ge(raw_ready[s], 16 * i + 16)
                    if not (isinstance(i, int) and i == 0):
                        act.wait_ge(projected, 2 * i + s - 1)
                    self.round_hi(raw, hi, s, hi_done)

                def evacuate(tile, s):
                    act.wait_ge(projected, tile + 1)
                    act.wait_ge(conv, STEPS * tile + 1)
                    nc.scalar.copy(pre[:, 3:3 + 2 * NW].rearrange("p (g r) -> p g r", r=NW),
                                   ps[:, 3 * s:3 * s + 2, 0:NW]).then_inc(pre_done, 1)
                    nc.scalar.copy(pre[:, 3 + 2 * NW:3 + ROWS_P], ps[:, 3 * s + 2, 0:256]).then_inc(pre_done, 1)
                    nc.scalar.copy(streams(pre)[:, :, 3:3 + SLEN],
                                   ps[:, 3 * s + 2, 256:384].rearrange("p (s t) -> p s t", t=SLEN)
                                   ).then_inc(pre_done, 1)

                def squash(tile):
                    act.wait_ge(conv, STEPS * tile + 5)
                    nc.scalar.activation(th[:, 0:A], acc[:, 0:A], ACT.Tanh, scale=0.5).then_inc(tanh_done, 1)

                split(0, 0)
                split(0, 1)
                evacuate(0, 0)
                squash(0)
                with act.Fori(1, TQ // 2) as i:
                    split(i, 0)
                    evacuate(2 * i - 1, 1)
                    squash(2 * i - 1)
                    split(i, 1)
                    evacuate(2 * i, 0)
                    squash(2 * i)
                evacuate(TQ - 1, 1)
                squash(TQ - 1)

            @block.vector
            def _(dve):
                nc.vector.memset(pre[:, 0:3], 0.0).then_inc(cleared, 1)
                dve.wait_ge(cleared, 1)
                dve.wait_ge(w8_split, 1)
                nc.vector.tensor_tensor(w8_lo[:, :, :], w8[:, :, :], w8_hi[:, :, :].bitcast(F32),
                                        ALU.subtract).then_inc(w8_split, 1)

                def rest(tile, s):
                    dve.wait_ge(hi_done, tile + 1)
                    self.take_lo(raw, hi, lo, s, lo_done)

                def convolve(tile):
                    tap = [self.vec[:, bass.ds(tile + V_CQ + w * TQ, 1)] for w in range(4)]
                    nc.vector.tensor_copy(streams(pre)[:, :, 0:3],
                                          self.hist_q[:, bass.ds(tile, 1), :].rearrange("p f (s t) -> p (f s) t", t=3)
                                          ).then_inc(conv, 1)
                    dve.wait_ge(pre_done, 3 * tile + 3)
                    dve.wait_ge(conv, STEPS * tile + 1)
                    nc.vector.tensor_scalar(acc[:, 0:A], pre[:, 0:A], tap[0], None, ALU.mult).then_inc(conv, 1)
                    for w in range(1, 4):
                        dve.wait_ge(conv, STEPS * tile + 1 + w)
                        nc.vector.scalar_tensor_tensor(acc[:, 0:A], pre[:, w:w + A], tap[w], acc[:, 0:A],
                                                       ALU.mult, ALU.add).then_inc(conv, 1)
                    tail = self.tail[:, bass.ds(tile, 1), :]
                    nc.vector.tensor_copy(tail[:, :, 0:3], pre[:, None, ROWS_P:ROWS_P + 3]).then_inc(conv, 1)
                    nc.vector.tensor_copy(tail[:, :, 3:27].rearrange("p f (s t) -> p (f s) t", t=3),
                                          streams(pre)[:, :, SLEN:SLEN + 3]).then_inc(conv, 1)
                    dve.wait_ge(tanh_done, tile + 1)
                    out = self.qkv[:, bass.ds(tile, 1), :]
                    nc.vector.scalar_tensor_tensor(out[:, :, 0:ROWS_P], th[:, None, 0:ROWS_P], 1.0,
                                                   acc[:, None, 0:ROWS_P], ALU.add, ALU.mult).then_inc(out_done, 1)
                    nc.vector.scalar_tensor_tensor(
                        out[:, :, ROWS_P:ROWS].rearrange("p f (s t) -> p (f s) t", t=SLEN),
                        streams(th)[:, :, 0:SLEN], 1.0, streams(acc)[:, :, 0:SLEN],
                        ALU.add, ALU.mult).then_inc(out_done, 1)

                rest(0, 0)
                rest(1, 1)
                convolve(0)
                with dve.Fori(1, TQ // 2) as i:
                    rest(2 * i, 0)
                    convolve(2 * i - 1)
                    rest(2 * i + 1, 1)
                    convolve(2 * i)
                convolve(TQ - 1)
                dve.wait_ge(ba_done, 1)
                nc.vector.tensor_copy(self.ba[:, :, :],
                                      ps[:, 6, 0:RT * 2 * H].rearrange("p (r c) -> p r c", c=2 * H)).then_inc(ba_out, 1)

            @block.tensor
            def _(pe):
                pe.wait_ge(w8_split, 2)
                for r in range(RT):
                    for k in range(KD):
                        for n, (x, w) in enumerate(((self.xn_hi, w8_hi), (self.xn_lo, w8_hi), (self.xn_hi, w8_lo))):
                            last = nc.tensor.matmul(ps[:, 6, r * 2 * H:(r + 1) * 2 * H], x[:, k, r * P:(r + 1) * P],
                                                    w[:, k, :], start=(k == 0 and n == 0),
                                                    stop=(k == KD - 1 and n == 2))
                last.then_inc(ba_done, 1)

                def tile(i, s):
                    pe.wait_ge(lo_done, 2 * i + s + 1)
                    if not (isinstance(i, int) and i == 0):
                        pe.wait_ge(pre_done, 6 * i + 3 * s - 3)
                    self.product(s, KD, lambda k: hi[:, s, k * P:(k + 1) * P], lambda k: lo[:, s, k * P:(k + 1) * P],
                                 self.xn_hi, self.xn_lo).then_inc(projected, 1)

                tile(0, 0)
                tile(0, 1)
                with pe.Fori(1, TQ // 2) as i:
                    tile(i, 0)
                    tile(i, 1)

    def states_out(self, width, tiles, prompt_out, sample_out):
        nc, ps = self.nc, self.ps
        n = width - 1
        m = n * (1 + STREAMS)
        back = self.at("state_rows", [m, tiles * P], F32, self.mem.t)
        turned, copied, stored = self.sems("turned", "copied", "stored")
        per = 4
        with nc.Block() as block:
            @block.tensor
            def _(pe):
                for f in range(tiles):
                    last = nc.tensor.transpose(ps[0:m, f // per, f % per * P:(f % per + 1) * P],
                                               self.tail[:, f, 0:m], self.ident)
                last.then_inc(turned, 1)

            @block.vector
            def _(dve):
                dve.wait_ge(turned, 1)
                nc.vector.tensor_copy(back[:, :].rearrange("p (b c) -> p b c", c=per * P),
                                      ps[0:m, 0:tiles // per, 0:per * P]).then_inc(copied, 1)

            @block.sync
            def _(sp):
                sp.wait_ge(copied, 1)
                sp.dma_start(prompt_out.rearrange("l b t c -> (l b t) c"), back[0:n, :]).then_inc(stored, 16)
                sp.dma_start(sample_out.rearrange("l s t c -> (l s t) c"), back[n:m, :]).then_inc(stored, 16)
                sp.wait_ge(stored, 32)

    def delta(self, a_log, dt_bias, state_delta, p_delta, s_delta):
        nc, ps, con, ba = self.nc, self.ps, self.con, self.ba
        at, t = self.at, [self.mem.t]

        def small(name, *free):
            a = at(name, [P, *free], F32, t[0])
            t[0] += -(-int(np.prod(free)) * 4 // 32) * 32
            return a

        square = [small("square0", ROWS), small("square1", ROWS)]
        names = ("tb", "beta", "xa", "ax", "y", "den", "rec", "sr", "s2", "poly", "sp", "g", "gc", "eg", "glc", "ekt",
                 "egl", "k_eps", "rk2", "sigma", "root", "vr", "q_eps", "osq", "f")
        v = {n: small(n, RT, H) for n in names}
        alog, dtb, ea = small("alog", H), small("dtb", H), small("ea", H)
        gseq, egls = small("gseq", STREAMS, H), small("egls", STREAMS, H)
        kst, qst, vst = small("kst", H, P), small("qst", H, P), small("vst", H, P)
        ug, dif, dec, dstr, egb = (small(n, H, P) for n in ("ug", "dif", "dec", "dstr", "egb"))
        ft, pt, qg = small("ft", H, P), small("pt", H, P), small("qg", H, P)
        kp, kt, vp = small("kp", H, P), small("kt", H, P), small("vp", H, P)
        ti, tt, yy, nwk, ww = (small(n, H, P) for n in ("ti", "tt", "yy", "nwk", "ww"))
        state = small("state", H, P)
        assert t[0] + H * STREAMS * P * 4 <= self.mem.h + RT * D * 4, (t[0] - self.mem.h)

        def over(col, chunk, cols=P):
            return v[col][:, chunk, :, None].to_broadcast([P, H, cols])

        (loaded, squared, summed, act_done, dve_done, pool_done, pe_done) = self.sems(
            "loaded", "squared", "summed", "act_done", "dve_done", "pool_done", "pe_done")
        with nc.Block() as block:
            @block.sync
            def _(sp):
                sp.dma_start(alog[:, :], a_log.to_broadcast([P, H])).then_inc(loaded, 16)
                sp.dma_start(dtb[:, :], dt_bias.to_broadcast([P, H])).then_inc(loaded, 16)

            @block.scalar
            def _(act):
                for f in range(2 * H):
                    if f >= 2:
                        act.wait_ge(summed, f - 1)
                    nc.scalar.activation(square[f % 2][:, :], self.qkv[:, f, :], ACT.Square).then_inc(squared, 1)
                nc.scalar.activation(v["tb"][:, :, :], ba[:, :, 0:H], ACT.Tanh, scale=0.5).then_inc(act_done, 1)
                act.wait_ge(loaded, 32)
                nc.scalar.activation(ea[:, :], alog[:, :], ACT.Exp).then_inc(act_done, 1)
                act.wait_ge(dve_done, 3)
                nc.scalar.activation(v["y"][:, :, :], v["ax"][:, :, :], ACT.Exp, scale=-1.0).then_inc(act_done, 1)
                act.wait_ge(pe_done, 1)
                act.wait_ge(dve_done, 22)
                nc.scalar.activation(v["eg"][:, :, :], v["gc"][:, :, :], ACT.Exp).then_inc(act_done, 1)
                nc.scalar.activation(v["ekt"][:, :, :], v["glc"][:, :, :], ACT.Exp).then_inc(act_done, 1)
                nc.scalar.activation(v["egl"][:, :, :], ps[:, 2, 0:RT * H].rearrange("p (r c) -> p r c", c=H),
                                     ACT.Exp).then_inc(act_done, 1)
                nc.scalar.activation(egls[:, :, :], ps[:, 3, 0:STREAMS * H].rearrange("p (r c) -> p r c", c=H),
                                     ACT.Exp).then_inc(act_done, 1)

            @block.gpsimd
            def _(pool):
                pool.wait_ge(dve_done, 24)
                nc.gpsimd.tensor_tensor(v["root"][:, :, :], v["k_eps"][:, :, :],
                                        self.half[:, 44:80].rearrange("p (r c) -> p r c", c=H),
                                        ALU.pow).then_inc(pool_done, 1)

            @block.vector
            def _(dve):
                n = [0]

                def step(ins):
                    n[0] += 1
                    ins.then_inc(dve_done, 1)
                    dve.wait_ge(dve_done, n[0])

                vv, tt_, ts_, stt = nc.vector, nc.vector.tensor_tensor, nc.vector.tensor_scalar, nc.vector.scalar_tensor_tensor
                al = {k: a[:, :, :] for k, a in v.items()}
                dve.wait_ge(loaded, 32)
                step(tt_(al["xa"], ba[:, :, H:2 * H], dtb[:, None, :].to_broadcast([P, RT, H]), ALU.add))
                step(ts_(al["sp"], al["xa"], -1.0, None, ALU.mult))
                step(tt_(al["ax"], al["xa"], al["sp"], ALU.max))
                dve.wait_ge(act_done, 3)
                step(ts_(al["den"], al["y"], 2.0, None, ALU.add))
                step(vv.reciprocal(al["rec"], al["den"]))
                step(tt_(al["sr"], al["y"], al["rec"], ALU.mult))
                step(tt_(al["s2"], al["sr"], al["sr"], ALU.mult))
                step(ts_(al["poly"], al["s2"], 1.0 / 17, None, ALU.mult))
                for k in (15, 13, 11, 9, 7, 5, 3):
                    step(stt(al["poly"], al["poly"], 1.0 / k, al["s2"], ALU.add, ALU.mult))
                step(stt(al["sp"], al["poly"], 1.0, al["sr"], ALU.add, ALU.mult))
                step(ts_(al["xa"], al["xa"], 0.0, -0.5, ALU.max, ALU.mult))
                step(tt_(al["sp"], al["xa"], al["sp"], ALU.subtract))
                step(stt(al["g"], al["sp"], 2.0, ea[:, None, :].to_broadcast([P, RT, H]), ALU.mult, ALU.mult))
                assert n[0] == 19, n
                step(tt_(gseq[:, :, :], con[:, C_SEQ:C_END, None].to_broadcast([P, STREAMS, H]),
                         v["g"][:, RT - 1, None, :].to_broadcast([P, STREAMS, H]), ALU.mult))
                dve.wait_ge(pe_done, 1)
                step(vv.tensor_copy(al["gc"], ps[:, 1, 0:RT * H].rearrange("p (r c) -> p r c", c=H)))
                step(tt_(al["glc"], ps[:, 2, 0:RT * H].rearrange("p (r c) -> p r c", c=H), al["gc"], ALU.subtract))
                dve.wait_ge(act_done, 1)
                step(ts_(al["beta"], al["tb"], 0.5, 0.5, ALU.mult, ALU.add))
                dve.wait_ge(summed, 2 * H)
                sums = ps[:, 0, 0:2 * H * RT].rearrange("p (h r) -> p r h", r=RT)
                step(ts_(al["k_eps"], sums[:, :, H:2 * H], 4 * EPS, None, ALU.add))
                step(ts_(al["q_eps"], sums[:, :, 0:H], 4 * EPS, P * EPS, ALU.add, ALU.mult))
                step(vv.reciprocal(al["rk2"], al["k_eps"]))
                step(tt_(al["sigma"], al["beta"], al["rk2"], ALU.mult))
                dve.wait_ge(pool_done, 1)
                step(ts_(al["vr"], al["root"], 0.5, None, ALU.mult))

            @block.tensor
            def _(pe):
                for f in range(2 * H):
                    pe.wait_ge(squared, f + 1)
                    for r in range(RT):
                        last = nc.tensor.matmul(ps[:, 0, f * RT + r:f * RT + r + 1], square[f % 2][:, r * P:(r + 1) * P],
                                                con[:, C_ONE:C_ONE + 1], start=True, stop=True)
                    last.then_inc(summed, 1)
                pe.wait_ge(dve_done, 20)
                gp = v["g"][:, 0:RT - 1, :].rearrange("p r c -> p (r c)")
                gs = v["g"][:, RT - 1, :]
                nc.tensor.matmul(ps[:, 1, 0:H * (RT - 1)], con[:, C_INC:C_INC + P], gp, start=True, stop=True)
                nc.tensor.matmul(ps[:, 1, H * (RT - 1):H * RT], con[:, C_INC + P:C_INC + 2 * P], gs, start=True, stop=True)
                nc.tensor.matmul(ps[:, 2, 0:H * (RT - 1)], self.ones, gp, start=True, stop=True)
                nc.tensor.matmul(ps[:, 2, H * (RT - 1):H * RT], con[:, C_BLK:C_BLK + P], gs, start=True, stop=True)
                nc.tensor.matmul(ps[:, 3, 0:STREAMS * H], self.ones, gseq[:, :, :].rearrange("p s c -> p (s c)"),
                                 start=True, stop=True).then_inc(pe_done, 1)

        B_KK, B_PP, B_GB, B_KR = 0, 1, 2, 3
        bank = lambda n: ps[:, n, :].rearrange("p (h c) -> p h c", c=P)

        def chunks(lo_chunk, hi_chunk, kind):
            levels = LEVELS_S if kind else LEVELS
            (staged, grown, dec_done, exp_done, strict, masked, prod1, prod2, ft_done, inputs, qg_done, t_init, lx, ly, lt,
             lc, lcd, wk_done, nwk_done, u_done, w_done, o_done, o_out, s_done, s_decayed, s_out, s_zero, stored) = self.sems(
                "staged", "grown", "dec_done", "exp_done", "strict", "masked", "prod1", "prod2", "ft_done", "inputs",
                "qg_done", "t_init", "level_x", "level_y", "level_t", "level_copied_a", "level_copied_d", "wk_done",
                "nwk_done", "u_done", "w_done", "o_done", "o_out", "s_done", "s_decayed", "s_out", "s_zero", "stored")
            tri = con[:, C_INC + kind * P:C_INC + (kind + 1) * P]
            neg = con[:, None, C_NEG + kind * P:C_NEG + (kind + 1) * P].to_broadcast([P, H, P])
            stri = con[:, None, C_STR + kind * P:C_STR + (kind + 1) * P].to_broadcast([P, H, P])
            idb = con[:, None, C_ID:C_ID + P].to_broadcast([P, H, P])
            qkv = self.qkv

            if kind:
                nwx = at("nwx", [P, STREAMS, P], F32, self.mem.t)
                wx = at("wx", [P, STREAMS, P], F32, self.mem.t + 4096)
                s_all = at("s_all", [P, H, STREAMS, P], F32, t[0])
                s_in, nwx_done, wx_done = self.sems("s_in", "nwx_done", "wx_done")
                heads = range(H)

            later = lambda i: not (isinstance(i, int) and i == 0)

            def loop(eng, body):
                body(0, lo_chunk)
                if hi_chunk - lo_chunk > 1:
                    with eng.Fori(1, hi_chunk - lo_chunk) as i:
                        body(i, i + lo_chunk)

            def part(which, n):
                return qkv[:, which * H:(which + 1) * H, bass.ds(n * P, P)]

            with nc.Block() as block:
                if kind:
                    @block.sync
                    def _(sp):
                        for h in heads:
                            sp.dma_start(s_all[:, h, :, :], state_delta[0, :, h].rearrange("s k v -> k s v")
                                         ).then_inc(s_in, 16)
                        for h in heads:
                            sp.wait_ge(s_out, 2 * h + 2)
                            sp.dma_start(s_delta[0, :, h].rearrange("s k v -> k s v"), s_all[:, h, :, :]
                                         ).then_inc(stored, 16)
                        sp.wait_ge(stored, 16 * H)
                else:
                    @block.sync
                    def _(sp):
                        sp.wait_ge(s_out, hi_chunk - lo_chunk)
                        sp.dma_start(p_delta[0, 0].rearrange("h k v -> k h v"), state[:, :, :]).then_inc(stored, 16)
                        sp.wait_ge(stored, 16)

                @block.gpsimd
                def _(pool):
                    if kind:
                        nc.gpsimd.memset(nwx[:, :, :], 0.0).then_inc(s_zero, 1)
                    else:
                        nc.gpsimd.memset(state[:, :, :], 0.0).then_inc(s_zero, 1)

                    def body(i, n):
                        if later(i):
                            pool.wait_ge(s_done, i)
                        nc.gpsimd.tensor_copy(kst[:, :, :], part(1, n)).then_inc(staged, 1)
                        nc.gpsimd.tensor_copy(qst[:, :, :], part(0, n)).then_inc(staged, 1)
                        nc.gpsimd.tensor_copy(vst[:, :, :], part(2, n)).then_inc(staged, 1)
                        nc.gpsimd.tensor_tensor(ug[:, :, :], tri[:, None, :].to_broadcast([P, H, P]),
                                                v["g"][:, bass.ds(n, 1), :].rearrange("p r (h o) -> p (r h) o", o=1)
                                                .to_broadcast([P, H, P]), ALU.mult).then_inc(grown, 1)
                        pool.wait_ge(dec_done, 2 * i + 1)
                        nc.gpsimd.tensor_tensor(dif[:, :, :], dif[:, :, :], neg, ALU.add).then_inc(masked, 1)
                        pool.wait_ge(exp_done, 2 * i + 2)
                        nc.gpsimd.tensor_tensor(dstr[:, :, :], dec[:, :, :], stri, ALU.mult).then_inc(strict, 1)
                        nc.gpsimd.tensor_tensor(qg[:, :, :], qst[:, :, :], egb[:, :, :], ALU.mult).then_inc(qg_done, 1)
                        pool.wait_ge(ft_done, 2 * i + 1)
                        nc.gpsimd.tensor_tensor(ft[:, :, :], idb, ft[:, :, :], ALU.subtract).then_inc(ft_done, 1)
                        if not kind:
                            pool.wait_ge(o_done, i + 1)
                            pool.wait_ge(s_zero, 1)
                            nc.gpsimd.tensor_tensor(state[:, :, :], state[:, :, :],
                                                    v["egl"][:, bass.ds(n, 1), :].rearrange("p r (h o) -> p (r h) o", o=1)
                                                    .to_broadcast([P, H, P]), ALU.mult).then_inc(s_decayed, 1)
                    loop(pool, body)

                @block.scalar
                def _(act):
                    def body(i, n):
                        act.wait_ge(prod1, 3 * i + 1)
                        act.wait_ge(dec_done, 2 * i + 1)
                        nc.scalar.activation(egb[:, :, :], bank(B_GB), ACT.Exp).then_inc(exp_done, 1)
                        act.wait_ge(masked, i + 1)
                        nc.scalar.activation(dec[:, :, :], dif[:, :, :], ACT.Exp).then_inc(exp_done, 1)
                        for l in range(levels):
                            act.wait_ge(lt, levels * i + l + 1)
                            nc.scalar.copy(ti[:, :, :], bank(B_PP)).then_inc(lc, 1)
                        act.wait_ge(wk_done, i + 1)
                        nc.scalar.activation(nwk[:, :, :], bank(B_KR), ACT.Copy, scale=-1.0).then_inc(nwk_done, 1)
                        act.wait_ge(o_done, i + 1)
                        nc.scalar.copy(part(0, n), bank(B_PP)).then_inc(o_out, 1)
                    loop(act, body)

                @block.vector
                def _(dve):
                    def per_row(name, n):
                        return v[name][:, bass.ds(n, 1), :].rearrange("p r (h o) -> p (r h) o", o=1).to_broadcast([P, H, P])

                    def body(i, n):
                        tensor = nc.vector.tensor_tensor
                        dve.wait_ge(prod1, 3 * i + 1)
                        tensor(dif[:, :, :], bank(B_GB), per_row("gc", n), ALU.subtract).then_inc(dec_done, 1)
                        nc.vector.tensor_copy(ti[:, :, :], idb).then_inc(t_init, 1)
                        nc.vector.tensor_copy(tt[:, :, :], idb).then_inc(t_init, 1)
                        dve.wait_ge(prod1, 3 * i + 2)
                        tensor(kp[:, :, :], bank(B_KR), per_row("eg", n), ALU.mult).then_inc(inputs, 1)
                        tensor(kt[:, :, :], bank(B_KR), per_row("ekt", n), ALU.mult).then_inc(inputs, 1)
                        dve.wait_ge(strict, i + 1)
                        tensor(ft[:, :, :], bank(B_KK), dstr[:, :, :], ALU.mult).then_inc(prod2, 1)
                        dve.wait_ge(prod2, i + 1)
                        tensor(ft[:, :, :], ft[:, :, :], per_row("sigma", n), ALU.mult).then_inc(ft_done, 1)
                        tensor(pt[:, :, :], bank(B_PP), dec[:, :, :], ALU.mult).then_inc(dec_done, 1)
                        dve.wait_ge(prod1, 3 * i + 3)
                        tensor(vp[:, :, :], bank(B_GB), per_row("vr", n), ALU.mult).then_inc(inputs, 1)
                        for l in range(levels):
                            lev = con[:, None, C_LEV + l * P:C_LEV + (l + 1) * P].to_broadcast([P, H, P])
                            dve.wait_ge(lx, levels * i + l + 1)
                            tensor(yy[:, :, :], bank(B_KK), lev, ALU.mult).then_inc(ly, 1)
                            dve.wait_ge(lt, levels * i + l + 1)
                            nc.vector.tensor_copy(tt[:, :, :], bank(B_GB)).then_inc(lcd, 1)
                        if not kind:
                            dve.wait_ge(u_done, i + 1)
                            tensor(ww[:, :, :], bank(B_KK), per_row("sigma", n), ALU.mult).then_inc(w_done, 1)
                            dve.wait_ge(s_done, i + 1)
                            dve.wait_ge(s_decayed, i + 1)
                            tensor(state[:, :, :], bank(B_GB), state[:, :, :], ALU.add).then_inc(s_out, 1)
                        else:
                            dve.wait_ge(nwk_done, 1)
                            dve.wait_ge(s_zero, 1)
                            for h in heads:
                                if h:
                                    dve.wait_ge(u_done, h)
                                diag = nwx[:, :, :].rearrange("p s c -> p (s c)")
                                for s in range(STREAMS):
                                    ins = nc.vector.tensor_copy(nwx[:, s, s * SLEN:(s + 1) * SLEN],
                                                                nwk[:, h, s * SLEN:(s + 1) * SLEN])
                                    ins.then_inc(nwx_done, 1)
                            dve.wait_ge(u_done, H)
                            tensor(ww[:, :, :], bank(B_KK), per_row("sigma", n), ALU.mult).then_inc(w_done, 1)
                            dve.wait_ge(w_done, 1)
                            for h in heads:
                                if h:
                                    dve.wait_ge(s_done, h)
                                tensor(wx[:, :, :], ww[:, h, None, :].to_broadcast([P, STREAMS, P]),
                                       con[:, C_SEQ:C_END, None].to_broadcast([P, STREAMS, P]), ALU.mult
                                       ).then_inc(wx_done, 1)
                                dve.wait_ge(o_done, 1)
                                if h:
                                    dve.wait_ge(s_out, 2 * h)
                                tensor(s_all[:, h, :, :], s_all[:, h, :, :],
                                       egls[:, :, h:h + 1].to_broadcast([P, STREAMS, P]), ALU.mult).then_inc(s_decayed, 1)
                                dve.wait_ge(s_decayed, h + 1)
                                dve.wait_ge(s_done, h + 1)
                                for x in range(2):
                                    tensor(s_all[:, h, 4 * x:4 * x + 4, :], s_all[:, h, 4 * x:4 * x + 4, :],
                                           bank(4 + x), ALU.add).then_inc(s_out, 1)
                    loop(dve, body)

                @block.tensor
                def _(pe):
                    def body(i, n):
                        mm = nc.tensor.matmul
                        if later(i):
                            pe.wait_ge(o_out, i)
                            pe.wait_ge(s_out, i)
                        pe.wait_ge(grown, i + 1)
                        mm(ps[:, B_GB, :], self.ones, ug[:, :, :].rearrange("p h c -> p (h c)"),
                           start=True, stop=True).then_inc(prod1, 1)
                        pe.wait_ge(staged, 3 * i + 3)
                        for h in range(H):
                            mm(bank(B_KK)[:, h, :], kst[:, h, :], kst[:, h, :], start=True, stop=True)
                            mm(bank(B_PP)[:, h, :], kst[:, h, :], qst[:, h, :], start=True, stop=True)
                        for h in range(H):
                            last = nc.tensor.transpose(bank(B_KR)[:, h, :], kst[:, h, :], self.ident)
                        last.then_inc(prod1, 1)
                        pe.wait_ge(exp_done, 2 * i + 1)
                        for h in range(H):
                            last = nc.tensor.transpose(bank(B_GB)[:, h, :], vst[:, h, :], self.ident)
                        last.then_inc(prod1, 1)
                        pe.wait_ge(t_init, 2 * i + 2)
                        pe.wait_ge(ft_done, 2 * i + 2)
                        pe.wait_ge(dec_done, 2 * i + 2)
                        pe.wait_ge(inputs, 3 * i + 3)
                        for l in range(levels):
                            if l:
                                pe.wait_ge(lc, levels * i + l)
                            for h in range(H):
                                last = mm(bank(B_KK)[:, h, :], ft[:, h, :], ti[:, h, :], start=True, stop=True)
                            last.then_inc(lx, 1)
                            if l:
                                pe.wait_ge(lcd, levels * i + l)
                            pe.wait_ge(ly, levels * i + l + 1)
                            for h in range(H):
                                mm(bank(B_PP)[:, h, :], tt[:, h, :], yy[:, h, :], start=True, stop=True)
                                last = mm(bank(B_GB)[:, h, :], yy[:, h, :], tt[:, h, :], start=True, stop=True)
                            last.then_inc(lt, 1)
                        pe.wait_ge(lcd, levels * i + levels)
                        for h in range(H):
                            last = mm(bank(B_KR)[:, h, :], kp[:, h, :], tt[:, h, :], start=True, stop=True)
                        last.then_inc(wk_done, 1)
                        pe.wait_ge(lc, levels * i + levels)
                        if not kind:
                            pe.wait_ge(s_zero, 1)
                            pe.wait_ge(nwk_done, i + 1)
                            for h in range(H):
                                mm(bank(B_KK)[:, h, :], tt[:, h, :], vp[:, h, :], start=True, stop=False)
                                last = mm(bank(B_KK)[:, h, :], nwk[:, h, :], state[:, h, :], start=False, stop=True)
                            last.then_inc(u_done, 1)
                            pe.wait_ge(w_done, i + 1)
                            pe.wait_ge(qg_done, i + 1)
                            for h in range(H):
                                mm(bank(B_PP)[:, h, :], state[:, h, :], qg[:, h, :], start=True, stop=False)
                                last = mm(bank(B_PP)[:, h, :], ww[:, h, :], pt[:, h, :], start=False, stop=True)
                            last.then_inc(o_done, 1)
                            for h in range(H):
                                last = mm(bank(B_GB)[:, h, :], kt[:, h, :], ww[:, h, :], start=True, stop=True)
                            last.then_inc(s_done, 1)
                        else:
                            for h in heads:
                                mm(bank(B_KK)[:, h, :], tt[:, h, :], vp[:, h, :], start=True, stop=False)
                                pe.wait_ge(s_in, 16 * H)
                                pe.wait_ge(nwx_done, STREAMS * (h + 1))
                                for s in range(STREAMS):
                                    last = mm(bank(B_KK)[:, h, :], nwx[:, s, :], s_all[:, h, s, :],
                                              start=False, stop=(s == STREAMS - 1))
                                last.then_inc(u_done, 1)
                            pe.wait_ge(w_done, 1)
                            pe.wait_ge(qg_done, 1)
                            for h in heads:
                                for s in range(STREAMS):
                                    mm(bank(B_PP)[:, h, s * SLEN:(s + 1) * SLEN], s_all[:, h, s, :],
                                       qg[:, h, s * SLEN:(s + 1) * SLEN], start=(s == 0), stop=False)
                                last = mm(bank(B_PP)[:, h, :], ww[:, h, :], pt[:, h, :], start=False, stop=True)
                            last.then_inc(o_done, 1)
                            for h in heads:
                                pe.wait_ge(wx_done, h + 1)
                                if h:
                                    pe.wait_ge(s_out, 2 * h)
                                for x in range(2):
                                    last = mm(ps[:, 4 + x, :], kt[:, h, :],
                                              wx[:, 4 * x:4 * x + 4, :].rearrange("p s v -> p (s v)"),
                                              start=True, stop=True)
                                last.then_inc(s_done, 1)
                    loop(pe, body)

        chunks(0, RT - 1, 0)
        chunks(RT - 1, RT, 1)

        diag = [kst, qst]
        (o_sq, o_sum, f_in, f_out, diag_done, spread, normed) = self.sems(
            "o_squared", "o_summed", "f_in", "f_out", "diag_done", "spread", "o_normed")
        o_all = self.qkv
        gain = self.vec[:, V_ON:V_ON + 1]
        with nc.Block() as block:
            @block.scalar
            def _(act):
                for h in range(H):
                    if h >= 2:
                        act.wait_ge(o_sum, h - 1)
                    nc.scalar.activation(square[h % 2][:, :], o_all[:, h, :], ACT.Square).then_inc(o_sq, 1)

            @block.gpsimd
            def _(pool):
                pool.wait_ge(f_in, 1)
                nc.gpsimd.tensor_tensor(v["f"][:, :, :], v["osq"][:, :, :],
                                        self.half[:, 0:36].rearrange("p (r c) -> p r c", c=H),
                                        ALU.pow).then_inc(f_out, 1)

            @block.vector
            def _(dve):
                dve.wait_ge(o_sum, H)
                nc.vector.scalar_tensor_tensor(v["osq"][:, :, :], ps[:, 0, 0:H * RT].rearrange("p (h r) -> p r h", r=RT),
                                               1.0 / P, v["q_eps"][:, :, :], ALU.mult, ALU.add).then_inc(f_in, 1)
                dve.wait_ge(f_out, 1)
                for r in range(RT + 1):
                    if r < RT:
                        if r >= 2:
                            dve.wait_ge(spread, r - 1)
                        nc.vector.tensor_tensor(diag[r % 2][:, :, :], self.ident[:, None, :].to_broadcast([P, H, P]),
                                                v["f"][:, r, :, None].to_broadcast([P, H, P]),
                                                ALU.mult).then_inc(diag_done, 1)
                    if r:
                        dve.wait_ge(spread, r)
                        rr = slice((r - 1) * P, r * P)
                        nc.vector.scalar_tensor_tensor(o_all[:, 0:H, rr], o_all[:, 0:H, rr], gain, bank(1 + (r - 1) % 2),
                                                       ALU.mult, ALU.mult).then_inc(normed, 1)

            @block.tensor
            def _(pe):
                for h in range(H):
                    pe.wait_ge(o_sq, h + 1)
                    for r in range(RT):
                        last = nc.tensor.matmul(ps[:, 0, h * RT + r:h * RT + r + 1], square[h % 2][:, r * P:(r + 1) * P],
                                                con[:, C_ONE:C_ONE + 1], start=True, stop=True)
                    last.then_inc(o_sum, 1)
                for r in range(RT):
                    pe.wait_ge(diag_done, r + 1)
                    if r >= 2:
                        pe.wait_ge(normed, r - 1)
                    nc.tensor.matmul(ps[:, 1 + r % 2, :], self.ones, diag[r % 2][:, :, :].rearrange("p h c -> p (h c)"),
                                     start=True, stop=True).then_inc(spread, 1)

    def gate_o(self, w_in):
        nc, ps = self.nc, self.ps
        t = self.mem.t
        raw, hi, lo = self.ring(2, t, t + 8192)
        th = self.at("th_z", [P, ROWS], F32, t + 24576)
        gated = self.at("gated", [P, ROWS], F32, t + 24576 + 4608)
        self.y_hi = self.at("ob_hi", [P, H, ROWS], F32R, self.mem.k)
        self.y_lo = self.at("ob_lo", [P, H, ROWS], F32R, self.mem.v)
        raw_ready = self.sems("raw_ready0", "raw_ready1")
        hi_done, lo_done, projected, tanh_done, silu, z_free, y_hi_done, y_lo_done = self.sems(
            "hi_done", "lo_done", "projected", "tanh_done", "silu", "gated_done", "y_hi_done", "y_lo_done")
        cols = w_in[0].rearrange("(k p) c -> p k c", p=P)
        wide = lambda a: a.rearrange("p (g r) -> p g r", r=NW)
        with nc.Block() as block:
            @block.sync
            def _(sp):
                for u in range(H):
                    if u >= 2:
                        sp.wait_ge(lo_done, u - 1)
                    sp.dma_start(raw[:, u % 2, :].rearrange("p (k c) -> p k c", c=P),
                                 cols[:, :, COL_Z + u * P:COL_Z + (u + 1) * P]).then_inc(raw_ready[u % 2], 16)

            @block.scalar
            def _(act):
                for u in range(H + 1):
                    if u < H:
                        act.wait_ge(raw_ready[u % 2], 16 * (u // 2) + 16)
                        if u >= 2:
                            act.wait_ge(projected, u - 1)
                        self.round_hi(raw, hi, u % 2, hi_done)
                    if u:
                        f = u - 1
                        act.wait_ge(projected, f + 1)
                        if f:
                            act.wait_ge(silu, f)
                        nc.scalar.activation(wide(th[:, :]), self.three(f % 2), ACT.Tanh, scale=0.5).then_inc(tanh_done, 1)
                        act.wait_ge(z_free, f + 1)
                        nc.scalar.activation(self.y_hi[:, f, :], gated[:, :], ACT.Copy, scale=0.5).then_inc(y_hi_done, 1)

            @block.vector
            def _(dve):
                for u in range(H + 1):
                    if u < H:
                        dve.wait_ge(hi_done, u + 1)
                        self.take_lo(raw, hi, lo, u % 2, lo_done)
                    if u:
                        f = u - 1
                        dve.wait_ge(tanh_done, f + 1)
                        if f:
                            dve.wait_ge(y_lo_done, f)
                        nc.vector.scalar_tensor_tensor(wide(gated[:, :]), wide(th[:, :]), 1.0, self.three(f % 2),
                                                       ALU.add, ALU.mult).then_inc(silu, 1)
                        dve.wait_ge(silu, f + 1)
                        nc.vector.tensor_tensor(gated[:, :], gated[:, :], self.qkv[:, f, :], ALU.mult
                                                ).then_inc(z_free, 1)
                        dve.wait_ge(y_hi_done, f + 1)
                        nc.vector.scalar_tensor_tensor(self.y_lo[:, f, :], gated[:, :], 0.5,
                                                       self.y_hi[:, f, :].bitcast(F32), ALU.mult, ALU.subtract
                                                       ).then_inc(y_lo_done, 1)

            @block.tensor
            def _(pe):
                for u in range(H):
                    pe.wait_ge(lo_done, u + 1)
                    if u >= 2:
                        pe.wait_ge(silu, u - 1)
                    self.product(u % 2, KD, lambda k: hi[:, u % 2, k * P:(k + 1) * P],
                                 lambda k: lo[:, u % 2, k * P:(k + 1) * P], self.xn_hi, self.xn_lo
                                 ).then_inc(projected, 1)

    def merge(self, branch, w_in, w_out):
        nc, ps = self.nc, self.ps
        first = branch == "b"
        col = COL_GB if first else COL_GA
        spare = self.mem.q if first else self.mem.v
        raw = self.at("g_raw", [P, 3, 1024], F32, spare)
        hi = self.at("g_hi", [P, 3, 1024], F32R, self.mem.t)
        lo = self.at("g_lo", [P, 3, 1024], F32R, self.mem.t + 12288)
        th = self.at("th_g", [P, ROWS], F32, spare + 12288)
        prod = self.at("gated_y", [P, ROWS], F32, self.mem.t + 24576)
        if first:
            self.mixed = self.at("mixed", [P, KD, ROWS], F32, self.mem.h)
        mixed = self.mixed
        raw_ready = self.sems("raw_ready0", "raw_ready1", "raw_ready2")
        hi_done = self.sems("hi_done0", "hi_done1", "hi_done2")
        lo_done = self.sems("lo_done0", "lo_done1", "lo_done2")
        gate_done, y_done, tanh_done, merged, gated = self.sems("gate_done", "y_done", "tanh_done", "merged", "gated")
        cols = w_in[0].rearrange("(k p) c -> p k c", p=P)
        outs = w_out[0].rearrange("(k p) c -> p k c", p=P)
        wide = lambda a: a.rearrange("p (g r) -> p g r", r=NW)
        N = KD // 2
        later = lambda i: not (isinstance(i, int) and i == 0)
        with nc.Block() as block:
            @block.sync
            def _(sp):
                def loads(i):
                    for s in (0, 2, 1):
                        if later(i):
                            sp.wait_ge(lo_done[s], i)
                        if s < 2:
                            dst = raw[:, s, :].rearrange("p (k c) -> p k c", c=P)
                            src = cols[:, :, bass.ds(i * (2 * P) + (col + s * P), P)]
                        else:
                            dst = raw[:, s, :].rearrange("p (k c) -> p k c", c=2 * P)
                            src = outs[:, :, bass.ds(i * (2 * P), 2 * P)]
                        sp.dma_start(dst, src).then_inc(raw_ready[s], 16)
                for i in range(N):
                    loads(i)

            @block.scalar
            def _(act):
                def split(i, s):
                    act.wait_ge(raw_ready[s], 16 * i + 16)
                    if later(i):
                        if s < 2:
                            act.wait_ge(gate_done, 2 * i + s - 1)
                        else:
                            act.wait_ge(y_done, 2 * i)
                    self.round_hi(raw, hi, s, hi_done[s])

                def squash(m, s):
                    act.wait_ge(gate_done, m + 1)
                    act.wait_ge(merged, m)
                    nc.scalar.activation(wide(th[:, :]), self.three(1), ACT.Tanh, scale=0.5).then_inc(tanh_done, 1)

                split(0, 0)
                split(0, 2)
                split(0, 1)
                squash(0, 0)
                with act.Fori(1, N) as i:
                    split(i, 0)
                    squash(2 * i - 1, 1)
                    split(i, 2)
                    split(i, 1)
                    squash(2 * i, 0)
                squash(KD - 1, 1)

            @block.vector
            def _(dve):
                def rest(i, s):
                    dve.wait_ge(hi_done[s], i + 1)
                    self.take_lo(raw, hi, lo, s, lo_done[s])

                def gate(m):
                    dve.wait_ge(tanh_done, m + 1)
                    dve.wait_ge(y_done, m + 1)
                    out = mixed[:, bass.ds(m, 1), :].rearrange("p f (g r) -> p (f g) r", r=NW)
                    if first:
                        nc.vector.scalar_tensor_tensor(out, wide(th[:, :]), 1.0, self.three(0), ALU.add, ALU.mult
                                                       ).then_inc(merged, 1)
                    else:
                        dve.wait_ge(gated, m)
                        nc.vector.scalar_tensor_tensor(wide(prod[:, :]), wide(th[:, :]), 1.0, self.three(0),
                                                       ALU.add, ALU.mult).then_inc(merged, 1)
                        dve.wait_ge(merged, m + 1)
                        nc.vector.tensor_tensor(out, out, wide(prod[:, :]), ALU.add).then_inc(gated, 1)

                rest(0, 0)
                rest(0, 2)
                rest(0, 1)
                gate(0)
                with dve.Fori(1, N) as i:
                    rest(i, 0)
                    gate(2 * i - 1)
                    rest(i, 2)
                    rest(i, 1)
                    gate(2 * i)
                gate(KD - 1)

            @block.tensor
            def _(pe):
                def pair(i):
                    for s in range(2):
                        pe.wait_ge(lo_done[s], i + 1)
                        if later(i) or s:
                            pe.wait_ge(tanh_done, 2 * i + s)
                        self.product(1, KD, lambda k: hi[:, s, k * P:(k + 1) * P],
                                     lambda k: lo[:, s, k * P:(k + 1) * P], self.xn_hi, self.xn_lo
                                     ).then_inc(gate_done, 1)
                        pe.wait_ge(lo_done[2], i + 1)
                        if later(i) or s:
                            pe.wait_ge(merged, 2 * i + s)
                        self.product(0, 4, lambda k: hi[:, 2, (2 * k + s) * P:(2 * k + s + 1) * P],
                                     lambda k: lo[:, 2, (2 * k + s) * P:(2 * k + s + 1) * P], self.y_hi, self.y_lo
                                     ).then_inc(y_done, 1)
                pair(0)
                with pe.Fori(1, N) as i:
                    pair(i)

    def branch_a(self, w_in):
        nc, ps = self.nc, self.ps
        L, S0 = padded(3)
        A = L - 2
        t = self.mem.t
        raw, hi, lo = self.ring(2, t, t + 8192)
        pre = self.at("pre_a", [P, L], F32, self.mem.v)
        acc = self.at("acc_a", [P, L], F32, self.mem.v + 4736)
        c_sb = self.at("c_sb", [P, ROWS], F32, self.mem.v + 2 * 4736)
        gated = self.at("gated_a", [P, ROWS], F32, t + 24576)
        self.tail = self.at("tail_a", [P, TA, 18], F32, self.mem.v + 2 * 4736 + 4608)
        self.y_hi = self.at("a_hi", [P, TA, ROWS], F32R, self.mem.q)
        self.y_lo = self.at("a_lo", [P, TA, ROWS], F32R, self.mem.k)
        raw_ready = self.sems("raw_ready0", "raw_ready1")
        hi_done, lo_done, projected, c_out, u_in, cleared, conv, out, y_hi_done, y_lo_done = self.sems(
            "hi_done", "lo_done", "projected", "c_out", "u_in", "cleared", "conv", "gated_out", "y_hi_done", "y_lo_done")
        cols = w_in[0].rearrange("(k p) c -> p k c", p=P)
        U = 3 * TA
        COLS = (WA, 2 * WA, 0)
        STEPS = 6

        def streams(buf, n=2 + SLEN):
            return buf[:, S0:L].rearrange("p (s t) -> p s t", t=n)

        def plain(a):
            return (a[:, 0:2 * NW].rearrange("p (g r) -> p g r", r=NW), a[:, 2 * NW:ROWS_P],
                    a[:, ROWS_P:ROWS].rearrange("p (s t) -> p s t", t=SLEN))

        def banks(s):
            return (ps[:, 3 * s:3 * s + 2, 0:NW], ps[:, 3 * s + 2, 0:256],
                    ps[:, 3 * s + 2, 256:384].rearrange("p (s t) -> p s t", t=SLEN))

        def convolved(buf, lead):
            return (buf[:, lead:lead + 2 * NW].rearrange("p (g r) -> p g r", r=NW), buf[:, lead + 2 * NW:lead + ROWS_P],
                    streams(buf)[:, :, lead:lead + SLEN])

        with nc.Block() as block:
            @block.sync
            def _(sp):
                for u in range(U):
                    if u >= 2:
                        sp.wait_ge(lo_done, u - 1)
                    c = COLS[u % 3] + u // 3 * P
                    sp.dma_start(raw[:, u % 2, :].rearrange("p (k c) -> p k c", c=P),
                                 cols[:, :, c:c + P]).then_inc(raw_ready[u % 2], 16)

            @block.scalar
            def _(act):
                for u in range(U + 1):
                    if u < U:
                        act.wait_ge(raw_ready[u % 2], 16 * (u // 2) + 16)
                        if u >= 2:
                            act.wait_ge(projected, u - 1)
                        self.round_hi(raw, hi, u % 2, hi_done)
                    if u % 3 == 1:
                        f = u // 3
                        act.wait_ge(projected, u)
                        if f:
                            act.wait_ge(u_in, 3 * f)
                        nc.scalar.copy(c_sb[:, :].rearrange("p (g r) -> p g r", r=NW), self.three((u - 1) % 2)
                                       ).then_inc(c_out, 1)
                    if u and u % 3 == 0:
                        f = u // 3 - 1
                        act.wait_ge(out, 3 * f + 3)
                        nc.scalar.copy(self.y_hi[:, f, :], gated[:, :]).then_inc(y_hi_done, 1)

            @block.vector
            def _(dve):
                nc.vector.memset(pre[:, 0:2], 0.0).then_inc(cleared, 1)
                dve.wait_ge(cleared, 1)
                for u in range(U + 1):
                    if u < U:
                        dve.wait_ge(hi_done, u + 1)
                        self.take_lo(raw, hi, lo, u % 2, lo_done)
                    f = (u - 1) // 3
                    if u and u % 3 == 2:
                        nc.vector.tensor_copy(streams(pre)[:, :, 0:2],
                                              self.hist_a[:, f, :].rearrange("p (s t) -> p s t", t=2)).then_inc(conv, 1)
                        dve.wait_ge(c_out, f + 1)
                        dve.wait_ge(projected, u)
                        for dst, c, x in zip(convolved(pre, 2), plain(c_sb), banks((u - 1) % 2)):
                            nc.vector.tensor_tensor(dst, c, x, ALU.mult).then_inc(u_in, 1)
                        dve.wait_ge(u_in, 3 * f + 3)
                        dve.wait_ge(conv, STEPS * f + 1)
                        tap = [self.vec[:, V_CA + w * TA + f:V_CA + w * TA + f + 1] for w in range(3)]
                        nc.vector.tensor_scalar(acc[:, 0:A], pre[:, 0:A], tap[0], None, ALU.mult).then_inc(conv, 1)
                        for w in range(1, 3):
                            dve.wait_ge(conv, STEPS * f + 1 + w)
                            nc.vector.scalar_tensor_tensor(acc[:, 0:A], pre[:, w:w + A], tap[w], acc[:, 0:A],
                                                           ALU.mult, ALU.add).then_inc(conv, 1)
                        nc.vector.tensor_copy(self.tail[:, f, 0:2], pre[:, ROWS_P:ROWS_P + 2]).then_inc(conv, 1)
                        nc.vector.tensor_copy(self.tail[:, f, 2:18].rearrange("p (s t) -> p s t", t=2),
                                              streams(pre)[:, :, SLEN:SLEN + 2]).then_inc(conv, 1)
                    if u and u % 3 == 0:
                        dve.wait_ge(projected, u)
                        dve.wait_ge(conv, STEPS * f + 4)
                        for dst, c, x in zip(plain(gated), convolved(acc, 0), banks((u - 1) % 2)):
                            nc.vector.tensor_tensor(dst, c, x, ALU.mult).then_inc(out, 1)
                        dve.wait_ge(y_hi_done, f + 1)
                        nc.vector.tensor_tensor(self.y_lo[:, f, :], gated[:, :], self.y_hi[:, f, :].bitcast(F32),
                                                ALU.subtract).then_inc(y_lo_done, 1)
                        dve.wait_ge(y_lo_done, f + 1)

            @block.tensor
            def _(pe):
                for u in range(U):
                    pe.wait_ge(lo_done, u + 1)
                    if u >= 2:
                        f, kind = (u - 2) // 3, (u - 2) % 3
                        pe.wait_ge((c_out, u_in, out)[kind], (f + 1, 3 * f + 3, 3 * f + 3)[kind])
                    self.product(u % 2, KD, lambda k: hi[:, u % 2, k * P:(k + 1) * P],
                                 lambda k: lo[:, u % 2, k * P:(k + 1) * P], self.xn_hi, self.xn_lo
                                 ).then_inc(projected, 1)

    def residual(self, w_o, x_prompt, x_sample):
        nc, ps = self.nc, self.ps
        mixed = self.mixed
        raw, hi, lo = self.ring(4, self.mem.v, self.mem.v + 16384)
        XB = 3
        x_buf = self.at("x_buf", [P, XB, 512], F32, self.mem.q)
        raw_ready = self.sems(*(f"raw_ready{s}" for s in range(4)))
        x_in = self.sems(*(f"x_in{s}" for s in range(XB)))
        mix_hi, mix_lo, hi_done, lo_done, tile_done, added = self.sems(
            "mix_hi", "mix_lo", "hi_done", "lo_done", "tile_done", "added")
        cols = w_o[0].rearrange("(u k p) c -> p u k c", p=P, k=2)
        with nc.Block() as block:
            @block.sync
            def _(sp):
                xs = 0

                def load_x(j):
                    half, r = divmod(j, RT)
                    if j >= XB:
                        sp.wait_ge(added, j - XB + 1)
                    src = x_prompt[0, r * P:(r + 1) * P] if r < RT - 1 else x_sample.rearrange("s t d -> (s t) d")
                    sp.dma_start(x_buf[:, j % XB, :], src[:, half * 512:(half + 1) * 512]).then_inc(x_in[j % XB], 16)

                for u in range(8):
                    if u >= 4:
                        sp.wait_ge(lo_done, u - 3)
                    sp.dma_start(raw[:, u % 4, :].rearrange("p (k c) -> p k c", c=512),
                                 cols[:, u % 4, :, u // 4 * 512:(u // 4 + 1) * 512]).then_inc(raw_ready[u % 4], 16)
                    if u == 3:
                        for j in range(XB):
                            load_x(j)
                for j in range(XB, 2 * RT):
                    load_x(j)

            @block.scalar
            def _(act):
                for f in range(KD):
                    nc.scalar.activation(self.xn_hi[:, f, :], mixed[:, f, :], ACT.Copy, scale=0.5).then_inc(mix_hi, 1)
                    if f % 2:
                        act.wait_ge(raw_ready[f // 2], 16)
                        self.round_hi(raw, hi, f // 2, hi_done)
                for u in range(4, 8):
                    act.wait_ge(raw_ready[u % 4], 32)
                    act.wait_ge(tile_done, RT)
                    self.round_hi(raw, hi, u % 4, hi_done)

            @block.vector
            def _(dve):
                for f in range(KD):
                    dve.wait_ge(mix_hi, f + 1)
                    nc.vector.scalar_tensor_tensor(self.xn_lo[:, f, :], mixed[:, f, :], 0.5,
                                                   self.xn_hi[:, f, :].bitcast(F32), ALU.mult, ALU.subtract
                                                   ).then_inc(mix_lo, 1)
                    if f % 2:
                        dve.wait_ge(hi_done, f // 2 + 1)
                        self.take_lo(raw, hi, lo, f // 2, lo_done)
                dve.wait_ge(mix_lo, KD)
                for j in range(2 * RT):
                    half, r = divmod(j, RT)
                    dve.wait_ge(tile_done, j + 1)
                    dve.wait_ge(x_in[j % XB], 16 * (j // XB) + 16)
                    nc.vector.tensor_tensor(self.rows[:, r, half * 512:(half + 1) * 512], ps[:, j % 6, :],
                                            x_buf[:, j % XB, :], ALU.add).then_inc(added, 1)
                    if j == RT - 1:
                        for u in range(4, 8):
                            dve.wait_ge(hi_done, u + 1)
                            self.take_lo(raw, hi, lo, u % 4, lo_done)

            @block.tensor
            def _(pe):
                pe.wait_ge(mix_lo, KD)
                for half in range(2):
                    pe.wait_ge(lo_done, 4 * half + 4)
                    for r in range(RT):
                        j = half * RT + r
                        if j >= 6:
                            pe.wait_ge(added, j - 5)
                        for k in range(KD):
                            w = slice(k % 2 * 512, k % 2 * 512 + 512)
                            for n, (x, y) in enumerate(((self.xn_hi, hi), (self.xn_lo, hi), (self.xn_hi, lo))):
                                last = nc.tensor.matmul(ps[:, j % 6, :], x[:, k, r * P:(r + 1) * P], y[:, k // 2, w],
                                                        start=(k == 0 and n == 0), stop=(k == KD - 1 and n == 2))
                        last.then_inc(tile_done, 1)

    def mlp(self, w_up, w_down):
        nc, ps = self.nc, self.ps
        raw, hi, lo = self.ring(4, self.mem.v, self.mem.v + 16384)
        act_t = self.at("relu", [P, ROWS], F32, self.mem.v + 49152)
        assert self.mem.v + 49152 + ROWS * 4 <= self.mem.h
        a_hi = self.at("hid_hi", [P, 4, ROWS], F32R, self.mem.q)
        a_lo = self.at("hid_lo", [P, 4, ROWS], F32R, self.mem.k)
        raw_ready = self.sems(*(f"raw_ready{s}" for s in range(4)))
        hi_done, lo_done, up_done, relu_done, squared, a_hi_done, a_lo_done, down_done, added = self.sems(
            "hi_done", "lo_done", "up_done", "relu_done", "squared", "a_hi_done",
            "a_lo_done", "down_done", "added")
        up = w_up[0].rearrange("(k p) c -> p k c", p=P)
        down = w_down[0].rearrange("(c k p) d -> p (c k) d", p=P, k=4)
        wide = lambda a: a.rearrange("p (g r) -> p g r", r=NW)
        later = lambda c: not (isinstance(c, int) and c == 0)
        with nc.Block() as block:
            @block.sync
            def _(sp):
                def load(c, u):
                    s = u % 4
                    if later(c) or u >= 4:
                        sp.wait_ge(lo_done, 8 * c + (u - 3))
                    if u < 4:
                        dst = raw[:, s, :].rearrange("p (k c) -> p k c", c=P)
                        src = up[:, :, bass.ds(c * FC + u * P, P)]
                    else:
                        dst = raw[:, s, :].rearrange("p (k c) -> p k c", c=512)
                        half, pair = divmod(u - 4, 2)
                        src = down[:, bass.ds(c * 4 + 2 * pair, 2), half * 512:(half + 1) * 512]
                    sp.dma_start(dst, src).then_inc(raw_ready[s], 16)

                for u in range(8):
                    load(0, u)
                with sp.Fori(1, NFC) as c:
                    for u in range(8):
                        load(c, u)

            @block.scalar
            def _(act):
                def split(c, u):
                    s = u % 4
                    act.wait_ge(raw_ready[s], 32 * c + (16 + 16 * (u // 4)))
                    if u >= 4:
                        act.wait_ge(up_done, 4 * c + (u - 3))
                    elif later(c):
                        act.wait_ge(down_done, 2 * RT * (c - 1) + (RT if u < 2 else 2 * RT))
                    self.round_hi(raw, hi, s, hi_done)

                def relu(c, j):
                    act.wait_ge(up_done, 4 * c + (j + 1))
                    if later(c) or j:
                        act.wait_ge(a_lo_done, 4 * c + j)
                    nc.scalar.activation(wide(act_t[:, :]), self.three(j % 2), ACT.Relu).then_inc(relu_done, 1)

                def round_act(c, j):
                    act.wait_ge(squared, 4 * c + (j + 1))
                    nc.scalar.copy(a_hi[:, j, :], act_t[:, :]).then_inc(a_hi_done, 1)

                def chunk(c, last):
                    for j in range(4):
                        relu(c, j)
                        split(c, 4 + j)
                        round_act(c, j)
                    if not last:
                        for u in range(4):
                            split(c + 1, u)

                for u in range(4):
                    split(0, u)
                chunk(0, False)
                with act.Fori(1, NFC - 1) as c:
                    chunk(c, False)
                chunk(NFC - 1, True)

            @block.vector
            def _(dve):
                def rest(c, u):
                    dve.wait_ge(hi_done, 8 * c + (u + 1))
                    self.take_lo(raw, hi, lo, u % 4, lo_done)

                def add(c, n):
                    half, r = divmod(n, RT)
                    out = self.rows[:, r, half * 512:(half + 1) * 512]
                    dve.wait_ge(down_done, 2 * RT * c + (n + 1))
                    nc.vector.tensor_tensor(out, ps[:, 6 + n % 2, :], out, ALU.add).then_inc(added, 1)

                def chunk(c, last):
                    for j in range(4):
                        dve.wait_ge(relu_done, 4 * c + (j + 1))
                        nc.vector.tensor_tensor(act_t[:, :], act_t[:, :], act_t[:, :], ALU.mult).then_inc(squared, 1)
                        rest(c, 4 + j)
                        dve.wait_ge(a_hi_done, 4 * c + (j + 1))
                        nc.vector.tensor_tensor(a_lo[:, j, :], act_t[:, :], a_hi[:, j, :].bitcast(F32), ALU.subtract
                                                ).then_inc(a_lo_done, 1)
                    for n in range(2 * RT):
                        add(c, n)
                        if not last and n in (RT - 1, 2 * RT - 1):
                            rest(c + 1, 2 * (n // RT))
                            rest(c + 1, 2 * (n // RT) + 1)

                for u in range(4):
                    rest(0, u)
                with dve.Fori(0, NFC - 1) as c:
                    chunk(c, False)
                chunk(NFC - 1, True)

            @block.tensor
            def _(pe):
                def down_part(n, ks):
                    half, r = divmod(n, RT)
                    for k in ks:
                        s = 2 * half + k // 2
                        w = slice(k % 2 * 512, k % 2 * 512 + 512)
                        for m, (x, y) in enumerate(((a_hi, hi), (a_lo, hi), (a_hi, lo))):
                            last = nc.tensor.matmul(ps[:, 6 + n % 2, :], x[:, k, r * P:(r + 1) * P], y[:, s, w],
                                                    start=(k == 0 and m == 0), stop=(k == 3 and m == 2))
                    return last

                def chunk(c):
                    for j in range(4):
                        pe.wait_ge(lo_done, 8 * c + (j + 1))
                        if j >= 2:
                            pe.wait_ge(relu_done, 4 * c + (j - 1))
                        elif later(c):
                            pe.wait_ge(relu_done, 4 * c + (j - 1))
                        self.product(j % 2, KD, lambda k: hi[:, j, k * P:(k + 1) * P],
                                     lambda k: lo[:, j, k * P:(k + 1) * P], self.xn_hi, self.xn_lo).then_inc(up_done, 1)
                    for half in range(2):
                        pe.wait_ge(lo_done, 8 * c + (6 + 2 * half))
                        base = half * RT
                        if half == 0:
                            pe.wait_ge(a_lo_done, 4 * c + 3)
                            if later(c):
                                pe.wait_ge(added, 2 * RT * c)
                            down_part(0, range(3))
                            down_part(1, range(3))
                            pe.wait_ge(a_lo_done, 4 * c + 4)
                            down_part(0, range(3, 4)).then_inc(down_done, 1)
                            down_part(1, range(3, 4)).then_inc(down_done, 1)
                        for r in range(2 if half == 0 else 0, RT):
                            n = base + r
                            pe.wait_ge(added, 2 * RT * c + (n - 1))
                            down_part(n, range(4)).then_inc(down_done, 1)

                chunk(0)
                with pe.Fori(1, NFC) as c:
                    chunk(c)

    def final(self, final_g, y_prompt, y_sample):
        nc, stat = self.nc, self.stat
        gain = self.at("gain", [P, D], F32, self.mem.xn)
        junk = self.at("junk_f", [P, D], F32, self.mem.xn + 4096)
        out = self.at("out", [P, RT, D], F32, self.mem.xn + 8192)
        loaded, squared, mean, rooted, done, stored = self.sems("loaded", "squared", "mean", "rooted", "normed", "stored")
        with nc.Block() as block:
            @block.sync
            def _(sp):
                sp.dma_start(gain[:, :], final_g[None, :].to_broadcast([P, D])).then_inc(loaded, 16)
                for r in range(RT):
                    sp.wait_ge(done, r + 1)
                    dst = y_prompt[0, r * P:(r + 1) * P] if r < RT - 1 else y_sample.rearrange("s t d -> (s t) d")
                    sp.dma_start(dst, out[:, r, :]).then_inc(stored, 16)
                sp.wait_ge(stored, 16 * RT)

            @block.scalar
            def _(act):
                for r in range(RT):
                    if r:
                        act.wait_ge(squared, r)
                    nc.scalar.activation(junk[:, :], self.rows[:, r, :], ACT.Square,
                                         accum_out=stat[:, 0, r:r + 1]).then_inc(squared, 1)

            @block.gpsimd
            def _(pool):
                for r in range(RT):
                    pool.wait_ge(mean, r + 1)
                    nc.gpsimd.tensor_tensor(stat[:, 2, r:r + 1], stat[:, 1, r:r + 1], self.half[:, 0:1],
                                            ALU.pow).then_inc(rooted, 1)

            @block.vector
            def _(dve):
                dve.wait_ge(loaded, 16)
                for r in range(RT + 1):
                    if r < RT:
                        dve.wait_ge(squared, r + 1)
                        nc.vector.tensor_scalar(stat[:, 1, r:r + 1], stat[:, 0, r:r + 1], 1.0 / D, EPS,
                                                ALU.mult, ALU.add).then_inc(mean, 1)
                    if r:
                        dve.wait_ge(rooted, r)
                        nc.vector.scalar_tensor_tensor(out[:, r - 1, :], self.rows[:, r - 1, :], stat[:, 2, r - 1:r],
                                                       gain[:, :], ALU.mult, ALU.mult).then_inc(done, 1)


_INS = ["x_prompt", "x_sample", "state_conv_a", "state_conv_qkv", "state_delta", "norm1_g", "w_in", "conv_a_w",
        "w_a_out", "conv_qkv_w", "a_log", "dt_bias", "onorm_g", "w_b_out", "w_o", "norm2_g", "w_up", "w_down",
        "final_g"]
_OUTS = [(1, ROWS_P, D), (STREAMS, SLEN, D), (1, 1, 2, WA), (1, 1, 3, WQKV), (1, 1, H, P, P),
         (1, STREAMS, 2, WA), (1, STREAMS, 3, WQKV), (1, STREAMS, H, P, P)]


def kernel(**inputs):
    import numpy as _np
    import concourse.bacc as _bacc
    from concourse import mybir as _mybir
    from concourse.bass_utils import run_bass_kernel_spmd as _run

    nc = _bacc.Bacc("TRN2", target_bir_lowering=False, num_devices=1)
    arrays, args = {}, []
    for name in _INS:
        arrays[f"in_{name}"] = _np.ascontiguousarray(inputs[name])
    arrays["in_table"] = constants()
    for name, a in arrays.items():
        args.append(nc.dram_tensor(name, a.shape, _mybir.dt.from_np(a.dtype), kind="ExternalInput").ap())
    for i, shape in enumerate(_OUTS):
        args.append(nc.dram_tensor(f"out_{i}", shape, _mybir.dt.float32, kind="ExternalOutput").ap())
    build(nc, *args)
    r = _run(nc, [arrays], core_ids=[0])
    return tuple(r.results[0][f"out_{i}"] for i in range(len(_OUTS)))
```
